# Optimizing a Trainium2 kernel written in Bass

```python
import jax, jax.numpy as jnp
from jax import lax
import numpy as np

D_MODEL = 1024
BATCH = 1
SEQ = 1024
DEPTH = 2

GRID_W = 64
CTX_LEN = 256
HEAD_DIM = 64
NA_HEADS = 4
GA_HEADS = 8
GA_KV_HEADS = 2
WA_HEADS = 4
WA_KV_HEADS = 2
D_MIX = (NA_HEADS + GA_HEADS + WA_HEADS) * HEAD_DIM
NA_WIN_ROWS = 8
NA_WIN_COLS = 16
WA_RADIUS = 128
Q_BLOCK = 128
D_FF = 2816
CONV_W = 3
ROPE_THETA = 10000.0
ROPE_PAIRS_PER_AXIS = HEAD_DIM // 4
EPS = 1e-6
N_MOD = 6

PROJ_SIZES = (NA_HEADS * HEAD_DIM, NA_HEADS * HEAD_DIM, NA_HEADS * HEAD_DIM,
              GA_HEADS * HEAD_DIM, GA_KV_HEADS * HEAD_DIM, GA_KV_HEADS * HEAD_DIM,
              WA_HEADS * HEAD_DIM, WA_KV_HEADS * HEAD_DIM, WA_KV_HEADS * HEAD_DIM)
PROJ_SPLITS = tuple(int(s) for s in np.cumsum(PROJ_SIZES)[:-1])
D_PROJ = int(sum(PROJ_SIZES))

kernel_name = "hymba_style_parallel_heads_dit_block"

def rmsnorm(x, g):
    xf = x.astype(jnp.float32)
    y = xf * lax.rsqrt(jnp.mean(xf * xf, axis=-1, keepdims=True) + EPS)
    return (y * g.astype(jnp.float32)).astype(x.dtype)

def modulate(h, shift, scale):
    return h * (1 + scale) + shift

def axial_rope(n_tokens):
    t = jnp.arange(n_tokens, dtype=jnp.int32)
    row = (t // GRID_W).astype(jnp.float32)
    col = (t % GRID_W).astype(jnp.float32)
    inv = ROPE_THETA ** (-jnp.arange(ROPE_PAIRS_PER_AXIS, dtype=jnp.float32) / ROPE_PAIRS_PER_AXIS)
    ang = jnp.concatenate([row[:, None] * inv, col[:, None] * inv], axis=-1)
    return jnp.cos(ang), jnp.sin(ang)

def apply_rope(x, cos, sin):
    xf = x.astype(jnp.float32)
    half = HEAD_DIM // 2
    x1, x2 = xf[..., :half], xf[..., half:]
    c = cos[None, :, None, :]
    s = sin[None, :, None, :]
    return jnp.concatenate([x1 * c - x2 * s, x1 * s + x2 * c], axis=-1).astype(x.dtype)

def dense_attn(q, k, v, sink=None):
    B, Lq, H, d = q.shape
    KVH = k.shape[2]
    G = H // KVH
    qg = q.reshape(B, Lq, KVH, G, d)
    s = jnp.einsum('bqkgd,bskd->bkgqs', qg, k).astype(jnp.float32) * (d ** -0.5)
    if sink is not None:
        sk = jnp.broadcast_to(sink.reshape(KVH, G)[None, :, :, None, None].astype(jnp.float32),
                              s.shape[:-1] + (1,))
        p = jax.nn.softmax(jnp.concatenate([s, sk], axis=-1), axis=-1)[..., :-1]
    else:
        p = jax.nn.softmax(s, axis=-1)
    o = jnp.einsum('bkgqs,bskd->bqkgd', p.astype(v.dtype), v)
    return o.reshape(B, Lq, H, d)

def neighbourhood_attn(q, k, v, kc, vc, rpb):
    B, S, H, d = q.shape
    rows = S // GRID_W
    kr = min(NA_WIN_ROWS, rows)
    kw = NA_WIN_COLS
    qg = q.reshape(B, rows, GRID_W, H, d)
    kg = k.reshape(B, rows, GRID_W, H, d)
    vg = v.reshape(B, rows, GRID_W, H, d)
    col = jnp.arange(GRID_W)
    col_idx = jnp.clip(col - kw // 2, 0, GRID_W - kw)[:, None] + jnp.arange(kw)[None]
    dc = col_idx - col[:, None]
    row = jnp.arange(rows)
    row_start = jnp.clip(row - kr // 2, 0, rows - kr)
    scale = d ** -0.5

    def one_row(args):
        r, rs, q_r = args
        k_nb = lax.dynamic_slice_in_dim(kg, rs, kr, axis=1)[:, :, col_idx]
        v_nb = lax.dynamic_slice_in_dim(vg, rs, kr, axis=1)[:, :, col_idx]
        dr = rs + jnp.arange(kr) - r
        bias = rpb[:, dr[:, None, None] + NA_WIN_ROWS - 1, dc[None] + NA_WIN_COLS - 1]
        bias = bias.transpose(0, 2, 1, 3).astype(jnp.float32)
        s_loc = jnp.einsum('bwhd,brwchd->bhwrc', q_r, k_nb).astype(jnp.float32) * scale + bias[None]
        s_loc = s_loc.reshape(B, H, GRID_W, kr * kw)
        s_ctx = jnp.einsum('bwhd,bchd->bhwc', q_r, kc).astype(jnp.float32) * scale
        p = jax.nn.softmax(jnp.concatenate([s_loc, s_ctx], axis=-1), axis=-1).astype(v.dtype)
        p_loc = p[..., :kr * kw].reshape(B, H, GRID_W, kr, kw)
        p_ctx = p[..., kr * kw:]
        return (jnp.einsum('bhwrc,brwchd->bwhd', p_loc, v_nb)
                + jnp.einsum('bhwc,bchd->bwhd', p_ctx, vc))

    o = lax.map(one_row, (row, row_start, qg.swapaxes(0, 1)))
    return o.swapaxes(0, 1).reshape(B, S, H, d)

def global_gqa(q, k, v, kc, vc):
    B, S, H, d = q.shape
    k_all = jnp.concatenate([k, kc], axis=1)
    v_all = jnp.concatenate([v, vc], axis=1)
    nb = S // Q_BLOCK
    qb = q.reshape(B, nb, Q_BLOCK, H, d).swapaxes(0, 1)
    o = lax.map(lambda qi: dense_attn(qi, k_all, v_all), qb)
    return o.swapaxes(0, 1).reshape(B, S, H, d)

def window_gqa(q, k, v, kc, vc, sink):
    B, S, H, d = q.shape
    KVH = k.shape[2]
    G = H // KVH
    nb = S // Q_BLOCK
    span = Q_BLOCK + 2 * WA_RADIUS
    pad = ((0, 0), (WA_RADIUS, WA_RADIUS), (0, 0), (0, 0))
    kp = jnp.pad(k, pad)
    vp = jnp.pad(v, pad)
    idx = (jnp.arange(nb) * Q_BLOCK)[:, None] + jnp.arange(span)[None]
    kb = kp[:, idx]
    vb = vp[:, idx]
    kpos = idx - WA_RADIUS
    qpos = jnp.arange(S).reshape(nb, Q_BLOCK)
    valid = ((jnp.abs(qpos[:, :, None] - kpos[:, None, :]) <= WA_RADIUS)
             & (kpos[:, None, :] >= 0) & (kpos[:, None, :] < S))
    qb = q.reshape(B, nb, Q_BLOCK, KVH, G, d)
    scale = d ** -0.5
    s_loc = jnp.einsum('bnqkgd,bnskd->bnkgqs', qb, kb).astype(jnp.float32) * scale
    s_loc = jnp.where(valid[None, :, None, None], s_loc, -jnp.inf)
    s_ctx = jnp.einsum('bnqkgd,bckd->bnkgqc', qb, kc).astype(jnp.float32) * scale
    s_sink = jnp.broadcast_to(sink.reshape(KVH, G)[None, None, :, :, None, None].astype(jnp.float32),
                              s_loc.shape[:-1] + (1,))
    p = jax.nn.softmax(jnp.concatenate([s_loc, s_ctx, s_sink], axis=-1), axis=-1).astype(v.dtype)
    L = kc.shape[1]
    o = (jnp.einsum('bnkgqs,bnskd->bnqkgd', p[..., :span], vb)
         + jnp.einsum('bnkgqc,bckd->bnqkgd', p[..., span:span + L], vc))
    return o.reshape(B, S, H, d)

def token_mix(h, hc, w_in, q_gain, k_gain, rpb, sink, w_out, cos, sin, with_ctx_out):
    B, S, _ = h.shape
    L = hc.shape[1]
    heads = lambda t: t.reshape(t.shape[:-1] + (-1, HEAD_DIM))
    qa, ka, va, qb, kb, vb, qw, kw, vw = [heads(t) for t in jnp.split(h @ w_in, PROJ_SPLITS, axis=-1)]
    qca, kca, vca, qcb, kcb, vcb, qcw, kcw, vcw = [heads(t) for t in jnp.split(hc @ w_in, PROJ_SPLITS, axis=-1)]
    qb = apply_rope(rmsnorm(qb, q_gain), cos, sin)
    kb = apply_rope(rmsnorm(kb, k_gain), cos, sin)
    kcb = rmsnorm(kcb, k_gain)
    qw = apply_rope(qw, cos, sin)
    kw = apply_rope(kw, cos, sin)
    oa = neighbourhood_attn(qa, ka, va, kca, vca, rpb)
    ob = global_gqa(qb, kb, vb, kcb, vcb)
    ow = window_gqa(qw, kw, vw, kcw, vcw, sink)
    out = jnp.concatenate([oa, ob, ow], axis=2).reshape(B, S, D_MIX) @ w_out
    if not with_ctx_out:
        return out, None
    oca = dense_attn(qca, kca, vca)
    ocb = dense_attn(rmsnorm(qcb, q_gain), kcb, vcb)
    ocw = dense_attn(qcw, kcw, vcw, sink)
    out_c = jnp.concatenate([oca, ocb, ocw], axis=2).reshape(B, L, D_MIX) @ w_out
    return out, out_c

def conv_ffn(h, w_up, conv_w, conv_b, w_down):
    a, b = jnp.split(h @ w_up, 2, axis=-1)
    n = a.shape[1]
    half = CONV_W // 2
    ap = jnp.pad(a, ((0, 0), (half, half), (0, 0)))
    a = sum(ap[:, j:j + n] * conv_w[j] for j in range(CONV_W)) + conv_b
    return (jax.nn.silu(a) * b) @ w_down

def setup_inputs(seed: int = 0) -> dict:
    key = jax.random.key(seed)
    ks = jax.random.split(key, 20)
    f32 = jnp.float32
    nrm = lambda k, shape, s: jax.random.normal(k, shape, f32) * s
    D = D_MODEL
    return {
        "x": nrm(ks[0], (BATCH, SEQ, D), 1.0),
        "c": nrm(ks[1], (BATCH, D), 1.0),
        "ctx": nrm(ks[2], (BATCH, CTX_LEN, D), 1.0),
        "c_ctx": nrm(ks[3], (D,), 1.0),
        "attn_norm": 1.0 + nrm(ks[4], (DEPTH, D), 0.05),
        "ffn_norm": 1.0 + nrm(ks[5], (DEPTH, D), 0.05),
        "w_mod": nrm(ks[6], (DEPTH, D, N_MOD * D), 0.5 * D ** -0.5),
        "b_mod": nrm(ks[7], (DEPTH, N_MOD * D), 0.02),
        "w_in": nrm(ks[8], (DEPTH, D, D_PROJ), D ** -0.5),
        "q_gain": 1.0 + nrm(ks[9], (DEPTH, HEAD_DIM), 0.05),
        "k_gain": 1.0 + nrm(ks[10], (DEPTH, HEAD_DIM), 0.05),
        "na_rpb": nrm(ks[11], (DEPTH, NA_HEADS, 2 * NA_WIN_ROWS - 1, 2 * NA_WIN_COLS - 1), 0.1),
        "wa_sink": nrm(ks[12], (DEPTH, WA_HEADS), 0.5),
        "w_out": nrm(ks[13], (DEPTH, D_MIX, D), D_MIX ** -0.5),
        "w_up": nrm(ks[14], (DEPTH, D, 2 * D_FF), D ** -0.5),
        "conv_w": nrm(ks[15], (DEPTH, CONV_W, D_FF), CONV_W ** -0.5),
        "conv_b": nrm(ks[16], (DEPTH, D_FF), 0.01),
        "w_down": nrm(ks[17], (DEPTH, D_FF, D), D_FF ** -0.5),
        "final_norm": 1.0 + nrm(ks[18], (D,), 0.05),
    }

def reference(x, c, ctx, c_ctx, attn_norm, ffn_norm, w_mod, b_mod, w_in, q_gain, k_gain,
              na_rpb, wa_sink, w_out, w_up, conv_w, conv_b, w_down, final_norm):
    S = x.shape[1]
    cos, sin = axial_rope(S)
    c_act = jax.nn.silu(c)
    cc_act = jax.nn.silu(c_ctx)
    cx = ctx
    for l in range(DEPTH):
        last = l == DEPTH - 1
        mx = (c_act @ w_mod[l] + b_mod[l])[:, None, :]
        mc = cc_act @ w_mod[l] + b_mod[l]
        sh_a, sc_a, gt_a, sh_f, sc_f, gt_f = jnp.split(mx, N_MOD, axis=-1)
        csh_a, csc_a, cgt_a, csh_f, csc_f, cgt_f = jnp.split(mc, N_MOD, axis=-1)
        h = modulate(rmsnorm(x, attn_norm[l]), sh_a, sc_a)
        hc = modulate(rmsnorm(cx, attn_norm[l]), csh_a, csc_a)
        o, oc = token_mix(h, hc, w_in[l], q_gain[l], k_gain[l], na_rpb[l], wa_sink[l], w_out[l],
                          cos, sin, not last)
        x = x + gt_a * o
        x = x + gt_f * conv_ffn(modulate(rmsnorm(x, ffn_norm[l]), sh_f, sc_f),
                                w_up[l], conv_w[l], conv_b[l], w_down[l])
        if not last:
            cx = cx + cgt_a * oc
            cx = cx + cgt_f * conv_ffn(modulate(rmsnorm(cx, ffn_norm[l]), csh_f, csc_f),
                                       w_up[l], conv_w[l], conv_b[l], w_down[l])
    return rmsnorm(x, final_norm)


_drawn_inputs = setup_inputs


def setup_inputs(seed=0):
    import zlib

    import numpy as np

    out = dict(_drawn_inputs(seed))
    spreads = {}
    factors = {'attn_norm': 8.0,
     'q_gain': 8.0,
     'k_gain': 8.0,
     'na_rpb': 8.0,
     'wa_sink': 8.0,
     'conv_b': 8.0}
    for name, (base, spread) in spreads.items():
        noise = np.random.default_rng([zlib.crc32(name.encode()), seed]).standard_normal(out[name].shape)
        drawn = base * np.exp(spread * noise) if base else spread * noise
        out[name] = __import__('jax').numpy.asarray(drawn.astype(out[name].dtype))
    for name, factor in factors.items():
        out[name] = (out[name] * factor).astype(out[name].dtype)
    return out
```

```python
from contextlib import ExitStack

import concourse.bass as bass
import numpy as np
from concourse import mybir

F32 = mybir.dt.float32
F32R = mybir.dt.float32r
ALU = mybir.AluOpType
ACT = mybir.ActivationFunctionType
AX = mybir.AxisListType

P = 128
D = 1024
KT = D // P
SEQ, CTX = 1024, 256
TOK = SEQ + CTX
DEPTH = 2
GRID_W = 64
HD = 64
NA_ROWS, NA_COLS = 8, 16
F = 2816
FT = F // P
N_MOD = 6
EPS = 1e-6
MASKED = -1.0e38
QSCALE = HD ** -0.5
CHUNKS = [(0, 512), (512, 512), (1024, 256)]
NQ = SEQ // P
NB = TOK // P
BT = 2 * NA_ROWS - 1
BC = 2 * NA_COLS - 1
BIW = 9

NA_Q, NA_K, NA_V = 0, 256, 512
GA_Q, GA_K, GA_V = 768, 1280, 1408
WA_Q, WA_K, WA_V = 1536, 1792, 1920
V_TILES = [(NA_V, NA_V + 64), (NA_V + 128, NA_V + 192), (GA_V, GA_V + 64), (WA_V, WA_V + 64)]
QK_TILES = ([(NA_Q + 128 * i, NA_Q + 128 * i + 64) for i in range(2)]
            + [(NA_K + 128 * i, NA_K + 128 * i + 64) for i in range(2)]
            + [(GA_Q + 64 * i, GA_Q + 64 * (i + 4)) for i in range(4)]
            + [(GA_K, GA_K + 64), (WA_K, WA_K + 64)]
            + [(WA_Q + 64 * i, WA_Q + 64 * (i + 2)) for i in range(2)])
QK_NA_Q, QK_NA_K, QK_GA_Q, QK_GA_K, QK_WA_K, QK_WA_Q = 0, 2, 4, 8, 9, 10
O_NA, O_GA, O_WA = 0, 2, 6
O_ROWS = ([(128 * i, 128 * i + 64) for i in range(2)]
          + [(256 + 64 * i, 256 + 64 * (i + 4)) for i in range(4)]
          + [(768 + 64 * i, 768 + 64 * (i + 2)) for i in range(2)])

CONSTS = {}
_at = 0
for _name, _n in (("ident", P), ("ones", P), ("block_ones", P), ("rotate", P), ("cos", SEQ),
                  ("sin", SEQ), ("col_mask", GRID_W), ("row_mask", BIW * GRID_W), ("wa_mask", 3 * P),
                  ("shift", 2 * GRID_W - 1)):
    CONSTS[_name] = (_at, _n)
    _at += _n
N_CONST = _at


def shape_constants():
    t = np.zeros((P, N_CONST), np.float32)

    def put(name, a):
        t[:, CONSTS[name][0]:CONSTS[name][0] + CONSTS[name][1]] = a
    p = np.arange(P)
    put("ident", np.eye(P))
    put("ones", 1.0)
    put("block_ones", p[:, None] // HD == p[None] // HD)
    rot = np.zeros((P, P), np.float32)
    for m in range(P):
        if m % HD < HD // 2:
            rot[m + HD // 2, m] = -1.0
        else:
            rot[m - HD // 2, m] = 1.0
    put("rotate", rot)
    tok = np.arange(SEQ)
    n = HD // 4
    inv = np.float32(10000.0) ** (-np.arange(n, dtype=np.float32) / np.float32(n))
    ang = np.concatenate([(tok // GRID_W).astype(np.float32)[:, None] * inv,
                          (tok % GRID_W).astype(np.float32)[:, None] * inv], -1)
    put("cos", np.cos(ang).T[p % (HD // 2)])
    put("sin", np.sin(ang).T[p % (HD // 2)])
    c, kc = (p % GRID_W)[:, None], np.arange(GRID_W)[None]
    first = np.clip(c - NA_COLS // 2, 0, GRID_W - NA_COLS)
    put("col_mask", np.where((kc >= first) & (kc < first + NA_COLS), 0.0, MASKED))
    row, j = (p // GRID_W)[:, None], np.arange(BIW)[None]
    put("row_mask", np.repeat(np.where((j >= row) & (j < row + NA_ROWS), 0.0, MASKED), GRID_W, 1))
    i, k = p[:, None], p[None]
    put("wa_mask", np.concatenate([np.where(k >= i, 0.0, MASKED), np.zeros((P, P)),
                                   np.where(k <= i, 0.0, MASKED)], 1))
    put("shift", np.arange(2 * GRID_W - 1)[None] == GRID_W - 1 + NA_COLS - 1 - p[:, None])
    return t


def const(a, name):
    return a["consts"][:, CONSTS[name][0]:CONSTS[name][0] + CONSTS[name][1]]


def program(nc, a):
    ctx = ExitStack()
    with ctx:
        KB = 1024
        base = (nc.sbuf_base + 63) // 64 * 64

        def at(name, off, shape, dt=F32):
            return nc.alloc_sbuf_tensor_at(name, [P] + shape, dt, offset=base + off)

        class Phase:

            def __enter__(self):
                self.stack, self.sems = ExitStack(), []
                phases.append(self)

            def __exit__(self, *error):
                if error[0] is None:
                    with nc.Block() as blk:
                        @blk.gpsimd
                        def _(g):
                            for s in self.sems:
                                g.sem_clear(s)
                    phases.pop()
                    self.stack.close()

        phases = []

        def sem(name):
            s = phases[-1].stack.enter_context(nc.semaphore(name))
            phases[-1].sems.append(s)
            return s

        ps = ctx.enter_context(nc.psum_tensor("ps", [P, 8, 512], F32))

        BIG, RING, XAT, QKAT, FIX = 0, 80 * KB, 104 * KB, 144 * KB, 204 * KB
        W4 = 4 * P * KT
        h_hi = at("h_hi", BIG, [KT, TOK], F32R)
        h_lo = at("h_lo", BIG + 40 * KB, [KT, TOK], F32R)
        o_hi = at("o_hi", BIG, [KT, TOK], F32R)
        o_lo = at("o_lo", BIG + 40 * KB, [KT, TOK], F32R)
        w_raw = at("w_raw", RING, [2, KT, P])
        w_hi = at("w_hi", RING + 2 * W4, [2, KT, P], F32R)
        w_lo = at("w_lo", RING + 4 * W4, [2, KT, P], F32R)
        x = at("x", XAT, [KT, TOK])
        qk = at("qk", QKAT, [12, TOK])
        rope_cos = at("rope_cos", XAT + 20 * KB, [SEQ])
        rope_sin = at("rope_sin", XAT + 24 * KB, [SEQ])
        rope_mat = at("rope_mat", XAT + 28 * KB, [P])
        head_ones = at("head_ones", XAT + 28 * KB + 512, [P])
        rt1 = at("rt1", RING, [TOK])
        rt2 = at("rt2", RING + 5 * KB, [TOK])
        v_tm = at("v_tm", XAT, [NB, 512])
        k_hi = at("k_hi", RING, [TOK], F32R)
        k_lo = at("k_lo", RING + 5 * KB, [TOK], F32R)
        v_hi = at("v_hi", RING + 10 * KB, [NB, P], F32R)
        v_lo = at("v_lo", RING + 15 * KB, [NB, P], F32R)
        q_hi = at("q_hi", RING + 20 * KB, [2, P], F32R)
        q_lo = at("q_lo", RING + 21 * KB, [2, P], F32R)
        o_tm = at("o_tm", RING + 22 * KB, [2, P])
        zeros = at("zeros", RING + 23 * KB, [CTX])
        prob = at("prob", XAT + 20 * KB, [2, TOK])
        pt_hi = at("pt_hi", XAT + 30 * KB, [NB, P], F32R)
        pt_lo = at("pt_lo", XAT + 35 * KB, [NB, P], F32R)
        bias_raw = at("bias_raw", BIG + 10 * KB, [4, BT, GRID_W])
        col_mask = at("col_mask", BIG + 26 * KB, [GRID_W])
        row_mask = at("row_mask", BIG + 27 * KB, [BIW * GRID_W])
        bias_e = at("bias_e", BIG + 50 * KB, [2, BT * GRID_W])
        bias_i = at("bias_i", BIG + 58 * KB, [2, BIW * GRID_W])
        rpb_in = at("rpb_in", BIG + 30 * KB, [BC])
        rpb_t = at("rpb_t", BIG + 30 * KB + 512, [4 * BT])
        shift = at("shift", BIG + 31 * KB, [2 * GRID_W - 1])
        wa_mask = at("wa_mask", BIG + 63 * KB, [3 * P])
        sq = at("sq", QKAT, [2, TOK])
        sq_sum = at("sq_sum", QKAT + 10 * KB, [TOK])
        rstd = at("rstd", QKAT + 15 * KB, [TOK])
        nt = at("nt", QKAT + 20 * KB, [2, TOK])
        ones = at("ones", QKAT + 30 * KB, [P])
        x_in = at("x_in", QKAT + 40 * KB, [2, D])
        x_out = at("x_out", QKAT + 40 * KB, [2, D])
        stage = at("stage", QKAT + 50 * KB, [4, P])
        wd_raw = at("wd_raw", QKAT, [D])
        wd_hi = at("wd_hi", QKAT + 4 * KB, [2, D], F32R)
        wd_lo = at("wd_lo", QKAT + 12 * KB, [2, D], F32R)
        u_hi = at("u_hi", QKAT + 20 * KB, [2, TOK], F32R)
        u_lo = at("u_lo", QKAT + 30 * KB, [2, TOK], F32R)
        a_pad = at("a_pad", QKAT + 40 * KB, [TOK + 3])
        conv = at("conv", QKAT + 45 * KB + 512, [TOK + 1])
        gate = at("gate", QKAT + 51 * KB, [TOK + 1])
        wm = at("wm", BIG, [4, KT, 512])
        ident = at("ident", FIX, [P])
        vec = at("vec", FIX + 512, [4, P])
        modv = at("modv", FIX + 2560, [DEPTH * 48, 2])
        moda = at("moda", FIX + 3328, [DEPTH * 4, KT])
        sink = at("sink", FIX + 3584, [DEPTH * 4])
        cact = at("cact", FIX + 3616, [KT, 2])
        stat = at("stat", FIX + 3680, [24])
        gq = at("gq", FIX + 3776, [2])

        x_spill = nc.dram_tensor("x_spill", [P, KT, TOK], F32)

        def load():
            s_const, s_stage, s_sink, s_zero = sem("s_const"), sem("s_stage"), sem("s_sink"), sem("s_zero")
            s_xin = [sem("s_xin0"), sem("s_xin1")]
            s_xt, s_xc, s_vt, s_vc = sem("s_xt"), sem("s_xc"), sem("s_vt"), sem("s_vc")
            s_wm = [sem(f"s_wm{r}") for r in range(4)]
            s_cact, s_modmm, s_modv = sem("s_cact"), sem("s_modmm"), sem("s_modv")
            NCH = DEPTH * 12
            wmod = a["w_mod"].rearrange("l (k p) n -> l p k n", p=P)

            with nc.Block() as blk:
                @blk.gpsimd
                def _(g):
                    g.memset(stage[:, :, :], 0.0).then_inc(s_zero, 1)

                @blk.sync
                def _(sp):
                    sp.dma_start(ident[:, :], a["consts"][:, 0:P]).then_inc(s_const, 16)
                    sp.wait_ge(s_zero, 1)
                    rows = [(0, 0, a["b_mod"].rearrange("l (r c) -> (l r) c", c=P)),
                            (0, 96, a["c"].rearrange("o (r c) -> (o r) c", c=P)),
                            (0, 104, a["c_ctx"].rearrange("(r c) -> r c", c=P)),
                            (0, 112, a["final_norm"].rearrange("(r c) -> r c", c=P)),
                            (1, 0, a["attn_norm"].rearrange("l (r c) -> (l r) c", c=P)),
                            (1, 16, a["ffn_norm"].rearrange("l (r c) -> (l r) c", c=P)),
                            (1, 32, a["conv_b"].rearrange("l (r c) -> (l r) c", c=P))]
                    for l in range(DEPTH):
                        rows.append((2 + l, 0, a["conv_w"][l].rearrange("t (r c) -> (t r) c", c=P)))
                    for s, r0, src in rows:
                        sp.dma_start(stage[r0:r0 + src.shape[0], s, :], src).then_inc(s_stage, 16)
                    for n, name in enumerate(("q_gain", "k_gain")):
                        for half in range(2):
                            sp.dma_start(stage[76 + 2 * n:78 + 2 * n, 1, HD * half:HD * half + HD], a[name])\
                                .then_inc(s_stage, 16)
                    sp.dma_start(sink[:, :], a["wa_sink"].rearrange("(o l) h -> o (l h)", o=1)
                                 .to_broadcast([P, DEPTH * 4])).then_inc(s_sink, 16)
                    for i in range(NB):
                        if i >= 2:
                            sp.wait_ge(s_xt, i - 1)
                        src = a["x"][i * P:(i + 1) * P, :] if i < NQ else a["ctx"][(i - NQ) * P:(i - NQ + 1) * P, :]
                        sp.dma_start(x_in[:, i % 2, :], src).then_inc(s_xin[i % 2], 16)
                    sp.wait_ge(s_sink, 16)

                @blk.scalar
                def _(act):
                    for r in range(4):
                        act.dma_start(wm[:, r], wmod[0, :, :, r * 512:(r + 1) * 512]).then_inc(s_wm[r], 16)
                    act.wait_ge(s_vc, 1)
                    act.activation(cact[:, :, :].rearrange("p k v -> p v k"),
                                   vec[:, 0, 96:112].rearrange("p (v k) -> p v k", v=2), ACT.Silu)\
                        .then_inc(s_cact, 1)
                    for q in range(4, NCH):
                        act.wait_ge(s_modmm, q - 3)
                        c = q % 12
                        act.dma_start(wm[:, q % 4], wmod[q // 12, :, :, c * 512:(c + 1) * 512])\
                            .then_inc(s_wm[q % 4], 16)

                @blk.tensor
                def _(pe):
                    pe.wait_ge(s_const, 16)
                    pe.wait_ge(s_stage, 16 * 13)
                    for s in range(4):
                        m = pe.transpose(ps[:, 4, s * P:(s + 1) * P], stage[:, s, :], ident[:, :])
                    m.then_inc(s_vt, 1)
                    for i in range(NB):
                        pe.wait_ge(s_xin[i % 2], 16 * (i // 2 + 1))
                        if i >= 2:
                            pe.wait_ge(s_xc, i - 1)
                        for k in range(KT):
                            m = pe.transpose(ps[:, 2 * (i % 2) + k // 4, (k % 4) * P:(k % 4 + 1) * P],
                                             x_in[:, i % 2, k * P:(k + 1) * P], ident[:, :])
                        m.then_inc(s_xt, 1)
                    pe.wait_ge(s_cact, 1)
                    for q in range(NCH):
                        pe.wait_ge(s_wm[q % 4], 16 * (q // 4 + 1))
                        for j in range(4):
                            for k in range(KT):
                                m = pe.matmul(ps[:, 5, (4 * q + j) * 2:(4 * q + j) * 2 + 2],
                                              wm[:, q % 4, k, j * P:(j + 1) * P], cact[:, k, :],
                                              start=(k == 0), stop=(k == KT - 1))
                        m.then_inc(s_modmm, 1)

                @blk.vector
                def _(dve):
                    dve.wait_ge(s_vt, 1)
                    dve.tensor_copy(vec[:, :, :], ps[:, 4, :].rearrange("p (s c) -> p s c", s=4)).then_inc(s_vc, 1)
                    for i in range(NB):
                        dve.wait_ge(s_xt, i + 1)
                        b = 2 * (i % 2)
                        dve.tensor_copy(x[:, :, i * P:(i + 1) * P],
                                        ps[:, b:b + 2, :].rearrange("p a (b c) -> p (a b) c", c=P)).then_inc(s_xc, 1)
                    dve.wait_ge(s_vc, 1)
                    dve.wait_ge(s_modmm, NCH)
                    mp = ps[:, 5, 0:DEPTH * 96].rearrange("p (n v) -> p n v", v=2)
                    for v in range(2):
                        dve.tensor_tensor(modv[:, :, v], mp[:, :, v], vec[:, 0, 0:96], ALU.add).then_inc(s_modv, 1)
                    dve.wait_ge(s_modv, 2)
                    for l in range(DEPTH):
                        for w in range(2):
                            for v in range(2):
                                r = l * 48 + (1 + 3 * w) * KT
                                gain = vec[:, 1, 16 * w + l * KT:16 * w + (l + 1) * KT]
                                dve.scalar_tensor_tensor(out=moda[:, (l * 2 + w) * 2 + v, :],
                                                         in0=modv[:, r:r + KT, v], scalar=1.0, in1=gain,
                                                         op0=ALU.add, op1=ALU.mult).then_inc(s_modv, 1)

        def norm(l, w, toks, spill=False, final=False):
            nm = f"n{l}{w}_"
            s_one, s_sqs, s_add, s_sum, s_ms, s_sqrt, s_rs, s_t, s_hi, s_lo, s_sp = [
                sem(nm + n) for n in ("one", "sq", "add", "sum", "ms", "sqrt", "rs", "t", "hi", "lo", "sp")]
            chunks = [c for c in CHUNKS if c[0] < toks]
            segs = [(0, SEQ, 0)] + ([(SEQ, CTX, 1)] if toks > SEQ else [])
            ns = len(segs)
            with nc.Block() as blk:
                @blk.sync
                def _(sp):
                    sp.dma_start(ones[:, :], const(a, "ones")).then_inc(s_one, 16)
                    if spill:
                        sp.dma_start(x_spill.ap(), x[:, :, :]).then_inc(s_sp, 16)
                        sp.wait_ge(s_sp, 16)
                    if final:
                        for i in range(NQ):
                            sp.wait_ge(s_lo, i + 1)
                            sp.dma_start(a["out"][i * P:(i + 1) * P, :], x_out[:, i % 2, :]).then_inc(s_sp, 16)
                            sp.wait_ge(s_sp, 16 * (i + 1))

                @blk.scalar
                def _(act):
                    for k in range(KT):
                        if k >= 2:
                            act.wait_ge(s_add, k - 1)
                        act.activation(sq[:, k % 2, 0:toks], x[:, k, 0:toks], ACT.Square).then_inc(s_sqs, 1)
                    for c, (t0, n) in enumerate(chunks):
                        act.wait_ge(s_ms, c + 1)
                        act.activation(rstd[:, t0:t0 + n], rstd[:, t0:t0 + n], ACT.Sqrt).then_inc(s_sqrt, 1)
                    if final:
                        return
                    for k in range(KT):
                        for i, (t0, n, v) in enumerate(segs):
                            act.wait_ge(s_t, ns * k + i + 1)
                            act.activation(h_hi[:, k, t0:t0 + n], nt[:, k % 2, t0:t0 + n], ACT.Identity,
                                           bias=modv[:, l * 48 + 3 * w * KT + k, v:v + 1]).then_inc(s_hi, 1)

                @blk.tensor
                def _(pe):
                    pe.wait_ge(s_one, 16)
                    pe.wait_ge(s_add, KT)
                    for c, (t0, n) in enumerate(chunks):
                        pe.matmul(ps[:, c, 0:n], ones[:, :], sq_sum[:, t0:t0 + n], start=True, stop=True)\
                            .then_inc(s_sum, 1)
                    if final:
                        pe.wait_ge(s_t, KT)
                        for i in range(NQ):
                            if i >= 2:
                                pe.wait_ge(s_lo, i - 1)
                            b = 4 + 2 * (i % 2)
                            for k in range(KT):
                                m = pe.transpose(ps[:, b + k // 4, (k % 4) * P:(k % 4 + 1) * P],
                                                 x[:, k, i * P:(i + 1) * P], ident[:, :])
                            m.then_inc(s_hi, 1)

                @blk.vector
                def _(dve):
                    for k in range(KT):
                        dve.wait_ge(s_sqs, k + 1)
                        if k == 0:
                            dve.tensor_copy(sq_sum[:, 0:toks], sq[:, 0, 0:toks]).then_inc(s_add, 1)
                        else:
                            dve.wait_ge(s_add, k)
                            dve.tensor_tensor(sq_sum[:, 0:toks], sq_sum[:, 0:toks], sq[:, k % 2, 0:toks],
                                              ALU.add).then_inc(s_add, 1)
                    for c, (t0, n) in enumerate(chunks):
                        dve.wait_ge(s_sum, c + 1)
                        dve.tensor_scalar(rstd[:, t0:t0 + n], ps[:, c, 0:n], 1.0 / D, EPS, ALU.mult,
                                          ALU.add).then_inc(s_ms, 1)
                    for c, (t0, n) in enumerate(chunks):
                        dve.wait_ge(s_sqrt, c + 1)
                        dve.reciprocal(rstd[:, t0:t0 + n], rstd[:, t0:t0 + n]).then_inc(s_rs, 1)
                    dve.wait_ge(s_rs, len(chunks))
                    if final:
                        for k in range(KT):
                            dve.scalar_tensor_tensor(out=x[:, k, 0:toks], in0=x[:, k, 0:toks],
                                                     scalar=vec[:, 0, 112 + k:113 + k], in1=rstd[:, 0:toks],
                                                     op0=ALU.mult, op1=ALU.mult).then_inc(s_t, 1)
                        for i in range(NQ):
                            dve.wait_ge(s_hi, i + 1)
                            if i >= 2:
                                dve.wait_ge(s_sp, 16 * (i - 1))
                            b = 4 + 2 * (i % 2)
                            dve.tensor_copy(x_out[:, i % 2, :], ps[:, b:b + 2, :].rearrange("p a c -> p (a c)"))\
                                .then_inc(s_lo, 1)
                        return
                    for k in range(KT + 1):
                        if k < KT:
                            if k >= 2:
                                dve.wait_ge(s_lo, ns * (k - 1))
                            for t0, n, v in segs:
                                dve.scalar_tensor_tensor(out=nt[:, k % 2, t0:t0 + n], in0=x[:, k, t0:t0 + n],
                                                         scalar=moda[:, (l * 2 + w) * 2 + v, k:k + 1],
                                                         in1=rstd[:, t0:t0 + n], op0=ALU.mult, op1=ALU.mult)\
                                    .then_inc(s_t, 1)
                        if k >= 1:
                            kk = k - 1
                            for i, (t0, n, v) in enumerate(segs):
                                dve.wait_ge(s_hi, ns * kk + i + 1)
                                dve.scalar_tensor_tensor(out=h_lo[:, kk, t0:t0 + n], in0=nt[:, kk % 2, t0:t0 + n],
                                                         scalar=modv[:, l * 48 + 3 * w * KT + kk, v:v + 1],
                                                         in1=h_hi[:, kk, t0:t0 + n].bitcast(F32),
                                                         op0=ALU.add, op1=ALU.subtract).then_inc(s_lo, 1)

        def three_pass(pe, out, wh, wl, mh, ml):
            n = len(wh)
            for p_, (w_, m_) in enumerate(((wh, mh), (wh, ml), (wl, mh))):
                for k in range(n):
                    m = pe.matmul(out, w_[k], m_[k], start=(p_ == 0 and k == 0), stop=(p_ == 2 and k == n - 1))
            return m

        class Tiles:

            def __init__(self, nm, chunks):
                self.raw = [sem(nm + "raw0"), sem(nm + "raw1")]
                self.hi, self.lo, self.mm, self.out = [sem(nm + n) for n in ("whi", "wlo", "mm", "out")]
                self.chunks, self.n = chunks, len(chunks)

            def split_hi(self, act, i, s, first=False):
                act.wait_ge(self.raw[s], 32 * i + 32)
                if not first:
                    act.wait_ge(self.mm, self.n * (2 * i + s - 1))
                act.activation(w_hi[:, s], w_raw[:, s], ACT.Copy).then_inc(self.hi, 1)

            def split_lo(self, dve, i, s):
                dve.wait_ge(self.hi, 2 * i + s + 1)
                dve.tensor_tensor(w_lo[:, s], w_raw[:, s], w_hi[:, s].bitcast(F32), ALU.subtract)\
                    .then_inc(self.lo, 1)

            def multiply(self, pe, i, s, mh, ml, first=False):
                pe.wait_ge(self.lo, 2 * i + s + 1)
                for c, (t0, n) in enumerate(self.chunks):
                    if not first:
                        pe.wait_ge(self.out, self.n * (2 * i + s - 2) + c + 1)
                    three_pass(pe, ps[:, 3 * s + c, 0:n], [w_hi[:, s, k, :] for k in range(KT)],
                               [w_lo[:, s, k, :] for k in range(KT)],
                               [mh[:, k, t0:t0 + n] for k in range(KT)],
                               [ml[:, k, t0:t0 + n] for k in range(KT)]).then_inc(self.mm, 1)

        def project_in(l):
            nm = f"p{l}_"
            t = Tiles(nm, CHUNKS)
            s_vtt, s_vtc, s_rope = sem(nm + "vtt"), sem(nm + "vtc"), sem(nm + "rope")
            s_qs, s_qm, s_q = sem(nm + "qs"), sem(nm + "qm"), sem(nm + "q")
            s_sqt, s_rot = sem(nm + "sqt"), sem(nm + "rot")
            cols = V_TILES + QK_TILES
            wv = a["w_in"][l].rearrange("(k p) n -> p k n", p=P)
            NG = len(cols) // 2
            with nc.Block() as blk:
                @blk.sync
                def _(sp):
                    for g, (c0, c1) in enumerate(cols):
                        if g >= 2:
                            sp.wait_ge(t.lo, g - 1)
                        s = g % 2
                        if c1 == c0 + HD:
                            parts = [(slice(0, 4), slice(0, P), c0), (slice(4, 8), slice(0, P), c0)]
                        else:
                            parts = [(slice(0, 8), slice(0, HD), c0), (slice(0, 8), slice(HD, P), c1)]
                        for ks, ds_, c in parts:
                            sp.dma_start(w_raw[:, s, ks, ds_], wv[:, ks, c:c + ds_.stop - ds_.start])\
                                .then_inc(t.raw[s], 16)
                    sp.dma_start(rope_cos[:, :], const(a, "cos")).then_inc(s_rope, 16)
                    sp.dma_start(rope_sin[:, :], const(a, "sin")).then_inc(s_rope, 16)
                    sp.dma_start(rope_mat[:, :], const(a, "rotate")).then_inc(s_rope, 16)
                    sp.dma_start(head_ones[:, :], const(a, "block_ones")).then_inc(s_rope, 16)

                @blk.tensor
                def _(pe):
                    for s in range(2):
                        t.multiply(pe, 0, s, h_hi, h_lo, first=True)
                    with pe.Fori(1, 3) as i:
                        for s in range(2):
                            t.multiply(pe, i, s, h_hi, h_lo)
                    for b in range(NB):
                        if b == 0:
                            pe.wait_ge(t.out, 4 * t.n)
                        if b >= 2:
                            pe.wait_ge(s_vtc, b - 1)
                        for j in range(4):
                            m = pe.transpose(ps[:, 6 + b % 2, j * P:(j + 1) * P],
                                             qk[:, 8 + j, b * P:(b + 1) * P], ident[:, :])
                        m.then_inc(s_vtt, 1)
                    with pe.Fori(3, NG) as i:
                        for s in range(2):
                            t.multiply(pe, i, s, h_hi, h_lo)

                @blk.scalar
                def _(act):
                    def copy_out(i, s, dst):
                        for c, (t0, n) in enumerate(CHUNKS):
                            act.wait_ge(t.mm, t.n * (2 * i + s) + c + 1)
                            act.activation(qk[:, dst, t0:t0 + n], ps[:, 3 * s + c:3 * s + c + 1, 0:n]
                                           if not isinstance(dst, int) else ps[:, 3 * s + c, 0:n], ACT.Copy)\
                                .then_inc(t.out, 1)
                    for s in range(2):
                        t.split_hi(act, 0, s, first=True)
                    for i in range(2):
                        for s in range(2):
                            copy_out(i, s, 8 + 2 * i + s)
                            t.split_hi(act, i + 1, s)
                    with act.Fori(2, 6) as i:
                        for s in range(2):
                            copy_out(i, s, bass.ds(2 * i + (s - 4), 1))
                            t.split_hi(act, i + 1, s)
                    act.wait_ge(s_vtt, NB)
                    with act.Fori(6, NG - 1) as i:
                        for s in range(2):
                            copy_out(i, s, bass.ds(2 * i + (s - 4), 1))
                            t.split_hi(act, i + 1, s)
                    for s in range(2):
                        copy_out(NG - 1, s, 2 * (NG - 1) + s - 4)

                @blk.vector
                def _(dve):
                    for i in range(3):
                        for s in range(2):
                            t.split_lo(dve, i, s)
                    for b in range(NB):
                        dve.wait_ge(s_vtt, b + 1)
                        dve.tensor_copy(v_tm[:, b, :], ps[:, 6 + b % 2, :]).then_inc(s_vtc, 1)
                        if b in (3, 7):
                            t.split_lo(dve, 3, b // 4)
                    with dve.Fori(4, NG) as i:
                        for s in range(2):
                            t.split_lo(dve, i, s)

            g_tiles = list(range(QK_GA_Q, QK_GA_K + 1))
            r_tiles = g_tiles + [QK_WA_K, QK_WA_Q, QK_WA_Q + 1]
            s_g, s_ms, s_sqrt, s_r, s_n, s_t1, s_t2 = [sem(nm + n) for n in ("g", "ms", "sr", "r", "n", "t1", "t2")]
            ng = len(g_tiles)
            with nc.Block() as blk:
                @blk.scalar
                def _(act):
                    for n_, tile in enumerate(g_tiles):
                        if n_ >= 1:
                            act.wait_ge(s_qm, 3 * n_)
                        act.activation(rt1[:, :], qk[:, tile, :], ACT.Square).then_inc(s_sqt, 1)
                        act.wait_ge(s_ms, n_ + 1)
                        act.activation(rt2[:, :], rt2[:, :], ACT.Sqrt).then_inc(s_sqrt, 1)

                @blk.tensor
                def _(pe):
                    pe.wait_ge(s_rope, 64)
                    for n_, tile in enumerate(g_tiles):
                        pe.wait_ge(s_sqt, n_ + 1)
                        if n_ >= 1:
                            pe.wait_ge(s_ms, n_)
                        for c, (t0, n) in enumerate(CHUNKS):
                            pe.matmul(ps[:, c, 0:n], head_ones[:, :], rt1[:, t0:t0 + n], start=True, stop=True)\
                                .then_inc(s_qm, 1)
                    pe.wait_ge(s_n, ng)
                    for n_, tile in enumerate(r_tiles):
                        if n_ >= 2:
                            pe.wait_ge(s_t2, n_ - 1)
                        for c in range(2):
                            m = pe.matmul(ps[:, 4 + 2 * (n_ % 2) + c, :], rope_mat[:, :],
                                          qk[:, tile, c * 512:(c + 1) * 512], start=True, stop=True)
                        m.then_inc(s_rot, 1)

                @blk.vector
                def _(dve):
                    for n_, tile in enumerate(g_tiles):
                        gain = vec[:, 1, 76 + l:77 + l] if n_ < ng - 1 else vec[:, 1, 78 + l:79 + l]
                        dve.wait_ge(s_qm, 3 * n_ + 3)
                        if n_ >= 1:
                            dve.wait_ge(s_n, n_)
                        dve.tensor_scalar(rt2[:, :], ps[:, 0:3, :].rearrange("p a c -> p (a c)")[:, 0:TOK],
                                          1.0 / HD, EPS, ALU.mult, ALU.add).then_inc(s_ms, 1)
                        dve.wait_ge(s_sqrt, n_ + 1)
                        dve.reciprocal(rt2[:, :], rt2[:, :]).then_inc(s_r, 1)
                        dve.wait_ge(s_r, n_ + 1)
                        dve.scalar_tensor_tensor(out=qk[:, tile, :], in0=qk[:, tile, :], scalar=gain,
                                                 in1=rt2[:, :], op0=ALU.mult, op1=ALU.mult).then_inc(s_n, 1)
                    dve.wait_ge(s_n, ng)
                    dve.wait_ge(s_rope, 64)
                    for n_, tile in enumerate(r_tiles):
                        b = 4 + 2 * (n_ % 2)
                        dve.wait_ge(s_rot, n_ + 1)
                        if n_ >= 1:
                            dve.wait_ge(s_t2, n_)
                        dve.tensor_tensor(rt1[:, 0:SEQ], ps[:, b:b + 2, :].rearrange("p a c -> p (a c)"),
                                          rope_sin[:, :], ALU.mult).then_inc(s_t1, 1)
                        dve.tensor_tensor(qk[:, tile, 0:SEQ], qk[:, tile, 0:SEQ], rope_cos[:, :], ALU.mult)\
                            .then_inc(s_t1, 1)
                        dve.wait_ge(s_t1, 2 * n_ + 2)
                        dve.tensor_tensor(qk[:, tile, 0:SEQ], qk[:, tile, 0:SEQ], rt1[:, 0:SEQ], ALU.add)\
                            .then_inc(s_t2, 1)

        NA, GA, WA = "na", "ga", "wa"

        def key_span(kind, t):
            if t >= NQ:
                return 0, 0, None
            if kind == GA:
                return 0, SEQ, None
            if kind == WA:
                lo, hi = max(t - 1, 0) * P, min(t + 2, NQ) * P
                return lo, hi - lo, ("wa", P if t == 0 else 0)
            if 2 <= t < NQ - 2:
                return (2 * t - 4) * GRID_W, BIW * GRID_W, ("i", 0)
            row = 0 if t < 2 else 8
            return row * GRID_W, NA_ROWS * GRID_W, ("e", (row - 2 * t + 7) * GRID_W)

        def attention(l, kind, q_tiles):
            nm = f"a{l}{kind}_"
            (s_kvh, s_kv, s_qh, s_ql, s_qk, s_mp, s_mx, s_ex, s_tr, s_ph, s_pl, s_pv, s_dn, s_ri, s_oe,
             s_ot, s_oh, s_ol, s_b, s_bm, s_z, s_bt, s_bc) = [sem(nm + n) for n in (
                 "kvh", "kv", "qh", "ql", "qk", "mp", "mx", "ex", "tr", "ph", "pl", "pv", "dn", "ri", "oe",
                 "ot", "oh", "ol", "b", "bm", "z", "bt", "bc")]
            pairs = {NA: 2, GA: 4, WA: 2}[kind]
            q0 = {NA: QK_NA_Q, GA: QK_GA_Q, WA: QK_WA_Q}[kind]
            o0 = {NA: O_NA, GA: O_GA, WA: O_WA}[kind]
            U = 2 * q_tiles
            span = [key_span(kind, u // 2) for u in range(U)]
            total = [n + CTX for _, n, _ in span]
            pieces, blocks, groups = [], [], []
            for lo, n, _ in span:
                pc, bl = [], []
                for k0, m, c in ((lo, n, 0), (SEQ, CTX, n)):
                    while m:
                        w_ = min(m, 512 - c % 512)
                        pc.append((c, w_, k0))
                        c, k0, m = c + w_, k0 + w_, m - w_
                for k0, m, c in ((lo, n, 0), (SEQ, CTX, n)):
                    for j in range(0, m, P):
                        bl.append((c + j, min(P, m - j), (k0 + j) // P))
                pieces.append(pc)
                blocks.append(bl)
                groups.append([list(range(j, min(j + 4, len(bl)))) for j in range(0, len(bl), 4)])
            g_at = [sum(len(groups[v]) for v in range(u)) for u in range(U + 1)]
            n_mp = [(2 if total[u] > 1024 else 1) if kind == GA else (2 if span[u][1] else 1) for u in range(U)]
            mp_at = [sum(n_mp[:u]) for u in range(U + 1)]
            n_dn = [1 if (kind == GA and total[u] > 1024) or kind == WA else 0 for u in range(U)]
            dn_at = [sum(n_dn[:u]) for u in range(U + 1)]
            n_ex = [(2 if total[u] > 1024 else 1) if kind == GA else (2 if kind == WA else 1) for u in range(U)]
            ex_at = [sum(n_ex[:u]) for u in range(U + 1)]

            def scores(u, c, n):
                if c >= 1024:
                    return ps[:, 4, (u % 2) * CTX + c - 1024:(u % 2) * CTX + c - 1024 + n]
                b = 2 * (u % 2)
                return ps[:, b:b + 2, :].rearrange("p a c -> p (a c)")[:, c:c + n]

            part, mx, nmx, s0, s1, den, rinv, skc = [stat[:, 2 * n:2 * n + 2] for n in range(8)]

            tick = stat[:, 16:17]

            def col(t_, u):
                return t_[:, u % 2:u % 2 + 1]

            def ot_after(u):
                return (u - 2) // 2 if u % 2 == 0 and u >= 2 else None

            def pt_runs(u, bl):
                ws = [blocks[u][b][1] for b in bl]
                out, k0 = [], 0
                for k in range(1, len(ws) + 1):
                    if k == len(ws) or ws[k] != ws[k0]:
                        out.append((k0, k, ws[k0]))
                        k0 = k
                return out

            once = kind != NA
            with nc.Block() as blk:
                @blk.sync
                def _(sp):
                    if kind == NA:
                        sp.dma_start(rpb_in[0:4 * BT, :], a["na_rpb"][l].rearrange("h r c -> (h r) c")).then_inc(s_b, 16)
                        sp.dma_start(shift[:, :], const(a, "shift")).then_inc(s_b, 16)
                        sp.dma_start(col_mask[:, :], const(a, "col_mask")).then_inc(s_b, 16)
                        sp.dma_start(row_mask[:, :], const(a, "row_mask")).then_inc(s_b, 16)
                        sp.dma_start(wa_mask[:, :], const(a, "wa_mask")).then_inc(s_b, 16)
                        sp.wait_ge(s_b, 16 * 5)

                @blk.scalar
                def _(act):
                    def kv_hi(i):
                        if kind == NA:
                            ksrc, vsrc = qk[:, bass.ds(QK_NA_K + i, 1), :], v_tm[:, :, bass.ds(i * P, P)]
                            act.activation(k_hi[:, :].rearrange("p (a c) -> p a c", a=1), ksrc, ACT.Copy).then_inc(s_kvh, 1)
                        else:
                            kt, vc = (QK_GA_K, 256) if kind == GA else (QK_WA_K, 384)
                            vsrc = v_tm[:, :, vc:vc + P]
                            act.activation(k_hi[:, :], qk[:, kt, :], ACT.Copy).then_inc(s_kvh, 1)
                        act.activation(v_hi[:, :, :], vsrc, ACT.Copy).then_inc(s_kvh, 1)

                    def q_part(i, t):
                        if t >= 2:
                            act.wait_ge(s_qk, i * U + 2 * t - 2)
                        act.activation(q_hi[:, t % 2:t % 2 + 1, :], qk[:, bass.ds(q0 + i, 1), t * P:(t + 1) * P],
                                       ACT.Copy, scale=QSCALE).then_inc(s_qh, 1)

                    def exp(i, u):
                        act.wait_ge(s_mx, i * U + u + 1)
                        if u >= 2:
                            act.wait_ge(s_tr, i * g_at[U] + g_at[u - 1])
                            act.wait_ge(s_ri, i * U + u - 1)
                        if kind == GA:
                            for c, n, acc in ((0, min(total[u], 1024), s0), (1024, total[u] - 1024, s1)):
                                if n > 0:
                                    act.activation(prob[:, u % 2, c:c + n], scores(u, c, n), ACT.Exp,
                                                   bias=col(nmx, u), accum_out=col(acc, u)).then_inc(s_ex, 1)
                        else:
                            if kind == WA:
                                act.activation(col(s1, u), col(skc, u), ACT.Exp, bias=col(nmx, u)).then_inc(s_ex, 1)
                            act.activation(prob[:, u % 2, 0:total[u]], prob[:, u % 2, 0:total[u]], ACT.Exp,
                                           bias=col(nmx, u), accum_out=col(s0, u)).then_inc(s_ex, 1)

                    def pt_part(i, u):
                        for g, bl in enumerate(groups[u]):
                            act.wait_ge(s_tr, i * g_at[U] + g_at[u] + g + 1)
                            if g == 0 and u >= 1:
                                act.wait_ge(s_pv, i * U + u)
                            last = None
                            for k0, k1, rows in pt_runs(u, bl):
                                m = act.activation(pt_hi[0:rows, bl[0] + k0:bl[0] + k1, :],
                                                   ps[0:rows, 5 + (g_at[u] + g) % 2, k0 * P:k1 * P]
                                                   .rearrange("p (b c) -> p b c", c=P), ACT.Copy)
                            m.then_inc(s_ph, 1)

                    def o_part(i, t):
                        act.wait_ge(s_ot, i * q_tiles + t + 1)
                        act.activation(o_hi[:, bass.ds(o0 + i, 1), t * P:(t + 1) * P],
                                       ps[:, 7:8, P:2 * P], ACT.Copy).then_inc(s_oh, 1)

                    if once:
                        kv_hi(0)
                    with act.Fori(0, pairs) as i:
                        if not once:
                            kv_hi(i)
                        q_part(i, 0)
                        q_part(i, 1)
                        exp(i, 0)
                        for u in range(U):
                            if u >= 1 and ot_after(u - 1) is not None:
                                o_part(i, ot_after(u - 1))
                            if u + 1 < U:
                                exp(i, u + 1)
                            if u % 2 == 1 and (u + 3) // 2 < q_tiles:
                                q_part(i, (u + 3) // 2)
                            pt_part(i, u)
                        o_part(i, q_tiles - 1)
                        act.wait_ge(s_ol, (i + 1) * q_tiles)

                @blk.tensor
                def _(pe):
                    def qk_product(i, u):
                        h0, t = HD * (u % 2), u // 2
                        pe.wait_ge(s_ql, i * q_tiles + t + 1)
                        if u >= 2:
                            if kind == GA:
                                pe.wait_ge(s_ex, i * ex_at[U] + ex_at[u - 1])
                            else:
                                pe.wait_ge(s_mx, i * U + u - 1)
                        for c, n, k0 in pieces[u]:
                            if c >= 1024 and u >= 1:
                                pe.wait_ge(s_ex, i * ex_at[U] + ex_at[u])
                            m = three_pass(pe, scores(u, c, n), [q_hi[h0:h0 + HD, t % 2, :]],
                                           [q_lo[h0:h0 + HD, t % 2, :]], [k_hi[h0:h0 + HD, k0:k0 + n]],
                                           [k_lo[h0:h0 + HD, k0:k0 + n]])
                        m.then_inc(s_qk, 1)

                    def transposes(i, u, gs):
                        for g in gs:
                            if g == 0:
                                pe.wait_ge(s_ex, i * ex_at[U] + ex_at[u + 1])
                            n_ = g_at[u] + g
                            if n_ >= 2:
                                pe.wait_ge(s_pl, i * g_at[U] + n_ - 1)
                            for k, b in reversed(list(enumerate(groups[u][g]))):
                                c, w_, _ = blocks[u][b]
                                m = pe.transpose(ps[0:w_, 5 + n_ % 2, k * P:(k + 1) * P],
                                                 prob[:, u % 2, c:c + w_], ident[:, :])
                            m.then_inc(s_tr, 1)

                    def value_product(i, u):
                        h0 = HD * (u % 2)
                        pe.wait_ge(s_pl, i * g_at[U] + g_at[u + 1])
                        if u >= 1:
                            pe.wait_ge(s_oe, i * U + u)
                        if u >= 1 and ot_after(u - 1) is not None:
                            pe.wait_ge(s_ol, i * q_tiles + ot_after(u - 1) + 1)
                        bl = blocks[u]
                        out = ps[:, 7, h0:h0 + HD]
                        for p_, (p_t, v_t) in enumerate(((pt_hi, v_hi), (pt_hi, v_lo), (pt_lo, v_hi))):
                            for b, (_, w_, vt) in enumerate(bl):
                                m = pe.matmul(out, p_t[0:w_, b, :], v_t[0:w_, vt, h0:h0 + HD],
                                              start=(p_ == 0 and b == 0), stop=(p_ == 2 and b == len(bl) - 1))
                        m.then_inc(s_pv, 1)

                    def turn_out(i, t):
                        pe.wait_ge(s_oe, i * U + 2 * t + 2)
                        pe.transpose(ps[:, 7, P:2 * P], o_tm[:, t % 2, :], ident[:, :]).then_inc(s_ot, 1)

                    if kind == NA:
                        pe.wait_ge(s_b, 16 * 5)
                        pe.transpose(ps[0:BC, 7, 0:4 * BT], rpb_in[0:4 * BT, :], ident[0:4 * BT, 0:4 * BT])\
                            .then_inc(s_bt, 1)
                        pe.wait_ge(s_bc, 1)
                        for c in range(GRID_W):
                            m = pe.matmul(ps[0:GRID_W, c // 8, (c % 8) * 4 * BT:(c % 8 + 1) * 4 * BT],
                                          shift[0:BC, GRID_W - 1 - c:2 * GRID_W - 1 - c], rpb_t[0:BC, :],
                                          start=True, stop=True)
                            if c % 8 == 7:
                                m.then_inc(s_bt, 1)
                        pe.wait_ge(s_bc, 2 + 2 * 8)
                    if once:
                        pe.wait_ge(s_kv, 2)
                    with pe.Fori(0, pairs) as i:
                        if not once:
                            pe.wait_ge(s_kv, 2 * (i + 1))
                        qk_product(i, 0)
                        qk_product(i, 1)
                        for u in range(U):
                            ng_ = len(groups[u])
                            transposes(i, u, range(min(2, ng_)))
                            if u + 2 < U:
                                qk_product(i, u + 2)
                            transposes(i, u, range(2, ng_))
                            value_product(i, u)
                            if ot_after(u) is not None:
                                turn_out(i, ot_after(u))
                        turn_out(i, q_tiles - 1)
                        pe.wait_ge(s_ol, (i + 1) * q_tiles)

                @blk.vector
                def _(dve):
                    def kv_lo(i):
                        n = 2 * i if kind == NA else 0
                        dve.wait_ge(s_kvh, n + 1)
                        if kind == NA:
                            dve.tensor_tensor(k_lo[:, :].rearrange("p (a c) -> p a c", a=1),
                                              qk[:, bass.ds(QK_NA_K + i, 1), :],
                                              k_hi[:, :].bitcast(F32).rearrange("p (a c) -> p a c", a=1),
                                              ALU.subtract).then_inc(s_kv, 1)
                            vsrc = v_tm[:, :, bass.ds(i * P, P)]
                        else:
                            kt, vc = (QK_GA_K, 256) if kind == GA else (QK_WA_K, 384)
                            dve.tensor_tensor(k_lo[:, :], qk[:, kt, :], k_hi[:, :].bitcast(F32), ALU.subtract)\
                                .then_inc(s_kv, 1)
                            vsrc = v_tm[:, :, vc:vc + P]
                        dve.wait_ge(s_kvh, n + 2)
                        dve.tensor_tensor(v_lo[:, :, :], vsrc, v_hi[:, :, :].bitcast(F32), ALU.subtract)\
                            .then_inc(s_kv, 1)

                    def q_part(i, t):
                        dve.wait_ge(s_qh, i * q_tiles + t + 1)
                        dve.scalar_tensor_tensor(out=q_lo[:, t % 2:t % 2 + 1, :],
                                                 in0=qk[:, bass.ds(q0 + i, 1), t * P:(t + 1) * P], scalar=QSCALE,
                                                 in1=q_hi[:, t % 2:t % 2 + 1, :].bitcast(F32), op0=ALU.mult,
                                                 op1=ALU.subtract).then_inc(s_ql, 1)

                    def maximum(i, u):
                        dve.wait_ge(s_qk, i * U + u + 1)
                        m0 = i * mp_at[U] + mp_at[u]
                        if u >= 2:
                            dve.wait_ge(s_ex, i * ex_at[U] + ex_at[u - 1])
                        if kind == GA:
                            n = min(total[u], 1024)
                            dve.tensor_reduce(col(part, u), scores(u, 0, n), AX.X, ALU.max).then_inc(s_mp, 1)
                            if total[u] > 1024:
                                dve.tensor_reduce(col(mx, u), scores(u, 1024, total[u] - 1024), AX.X, ALU.max)\
                                    .then_inc(s_mp, 1)
                                dve.wait_ge(s_mp, m0 + 2)
                                dve.tensor_scalar(col(nmx, u), col(part, u), col(mx, u), -1.0, ALU.max, ALU.mult)\
                                    .then_inc(s_mx, 1)
                            else:
                                dve.wait_ge(s_mp, m0 + 1)
                                dve.tensor_scalar(col(nmx, u), col(part, u), -1.0, None, ALU.mult).then_inc(s_mx, 1)
                            return
                        lo, n, bias = span[u]
                        if u >= 2:
                            dve.wait_ge(s_tr, i * g_at[U] + g_at[u - 1])
                        dve.memset(tick, 0.0)
                        init = MASKED if kind == NA else col(skc, u)
                        if n:
                            if bias[0] == "wa":
                                b_ap = wa_mask[:, bias[1]:bias[1] + n]
                            else:
                                b_ap = (bias_e if bias[0] == "e" else bias_i)[:, u % 2, bias[1]:bias[1] + n]
                            dve.tensor_tensor_reduce(prob[:, u % 2, 0:n], scores(u, 0, n), b_ap, 1.0, MASKED,
                                                     ALU.add, ALU.max, col(part, u)).then_inc(s_mp, 1)
                        dve.tensor_tensor_reduce(prob[:, u % 2, n:n + CTX], scores(u, n, CTX), zeros[:, :], 1.0,
                                                 init, ALU.add, ALU.max, col(mx, u)).then_inc(s_mp, 1)
                        dve.wait_ge(s_mp, m0 + n_mp[u])
                        if n:
                            dve.tensor_scalar(col(nmx, u), col(part, u), col(mx, u), -1.0, ALU.max, ALU.mult)\
                                .then_inc(s_mx, 1)
                        else:
                            dve.tensor_scalar(col(nmx, u), col(mx, u), -1.0, None, ALU.mult).then_inc(s_mx, 1)

                    def pt_part(i, u):
                        for g, bl in enumerate(groups[u]):
                            n_ = g_at[u] + g
                            dve.wait_ge(s_ph, i * g_at[U] + n_ + 1)
                            for k0, k1, rows in pt_runs(u, bl):
                                m = dve.tensor_tensor(pt_lo[0:rows, bl[0] + k0:bl[0] + k1, :],
                                                      ps[0:rows, 5 + n_ % 2, k0 * P:k1 * P]
                                                      .rearrange("p (b c) -> p b c", c=P),
                                                      pt_hi[0:rows, bl[0] + k0:bl[0] + k1, :].bitcast(F32),
                                                      ALU.subtract)
                            m.then_inc(s_pl, 1)

                    def inverse(i, u):
                        dve.wait_ge(s_ex, i * ex_at[U] + ex_at[u + 1])
                        if u >= 2:
                            dve.wait_ge(s_oe, i * U + u - 1)
                        if n_dn[u]:
                            dve.tensor_scalar(col(den, u), col(s0, u), col(s1, u), None, ALU.add).then_inc(s_dn, 1)
                            dve.wait_ge(s_dn, i * dn_at[U] + dn_at[u + 1])
                            dve.reciprocal(col(rinv, u), col(den, u)).then_inc(s_ri, 1)
                        else:
                            dve.reciprocal(col(rinv, u), col(s0, u)).then_inc(s_ri, 1)

                    def scale_out(i, u):
                        t, h0 = u // 2, HD * (u % 2)
                        dve.wait_ge(s_pv, i * U + u + 1)
                        dve.wait_ge(s_ri, i * U + u + 1)
                        if ot_after(u) is not None:
                            dve.wait_ge(s_oh, i * q_tiles + ot_after(u) + 1)
                        dve.tensor_scalar(o_tm[:, t % 2, h0:h0 + HD], ps[:, 7, h0:h0 + HD], col(rinv, u), None,
                                          ALU.mult).then_inc(s_oe, 1)

                    def o_part(i, t):
                        dve.wait_ge(s_oh, i * q_tiles + t + 1)
                        dve.tensor_tensor(o_lo[:, bass.ds(o0 + i, 1), t * P:(t + 1) * P], ps[:, 7:8, P:2 * P],
                                          o_hi[:, bass.ds(o0 + i, 1), t * P:(t + 1) * P].bitcast(F32),
                                          ALU.subtract).then_inc(s_ol, 1)

                    if kind == NA:
                        dve.wait_ge(s_bt, 1)
                        dve.tensor_copy(rpb_t[0:BC, :], ps[0:BC, 7, 0:4 * BT]).then_inc(s_bc, 1)
                        dve.memset(bias_raw[GRID_W:P, :, 0, :], MASKED).then_inc(s_bc, 1)
                        for b in range(8):
                            src = ps[0:GRID_W, b, 0:8 * 4 * BT].rearrange("p (c h r) -> p h r c", c=8, h=4)
                            dve.wait_ge(s_bt, b + 2)
                            for h in range(2):
                                for hd in range(4):
                                    m = dve.tensor_copy(bias_raw[GRID_W * h:GRID_W * h + GRID_W, hd, h:BT,
                                                                 8 * b:8 * b + 8], src[:, hd, 0:BT - h, :])
                                m.then_inc(s_bc, 1)
                        dve.wait_ge(s_bc, 2 + 2 * 8)
                    if kind != GA:
                        dve.memset(zeros[:, :], 0.0).then_inc(s_z, 1)
                        dve.wait_ge(s_z, 1)
                    if once:
                        kv_lo(0)
                    with dve.Fori(0, pairs) as i:
                        if kind == NA:
                            kv_lo(i)
                            for h in range(2):
                                dve.tensor_tensor(bias_e[:, h, :].rearrange("p (a b c) -> p a b c", a=1, c=GRID_W),
                                                  bias_raw[:, bass.ds(2 * i + h, 1), :, :],
                                                  col_mask[:, :].rearrange("p (a b c) -> p a b c", a=1, b=1)
                                                  .to_broadcast([P, 1, BT, GRID_W]), ALU.add).then_inc(s_bm, 1)
                            dve.wait_ge(s_bm, 4 * i + 2)
                            for h in range(2):
                                dve.tensor_tensor(bias_i[:, h, :], bias_e[:, h, 3 * GRID_W:(3 + BIW) * GRID_W],
                                                  row_mask[:, :], ALU.add).then_inc(s_bm, 1)
                            dve.wait_ge(s_bm, 4 * i + 4)
                        if kind == WA:
                            for h in range(2):
                                dve.tensor_copy(skc[:, h:h + 1], sink[:, bass.ds(i + (l * 4 + 2 * h), 1)])\
                                    .then_inc(s_bm, 1)
                            dve.wait_ge(s_bm, 2 * i + 2)
                        q_part(i, 0)
                        q_part(i, 1)
                        maximum(i, 0)
                        maximum(i, 1)
                        inverse(i, 0)
                        for u in range(U):
                            if u >= 1:
                                scale_out(i, u - 1)
                                if ot_after(u - 1) is not None:
                                    o_part(i, ot_after(u - 1))
                            if u % 2 == 1 and (u + 3) // 2 < q_tiles:
                                q_part(i, (u + 3) // 2)
                            pt_part(i, u)
                            if u + 2 < U:
                                maximum(i, u + 2)
                            if u + 1 < U:
                                inverse(i, u + 1)
                        scale_out(i, U - 1)
                        o_part(i, q_tiles - 1)
                        dve.wait_ge(s_ol, (i + 1) * q_tiles)

        def project_out(l, toks):
            nm = f"w{l}_"
            chunks = [c for c in CHUNKS if c[0] < toks]
            t = Tiles(nm, chunks)
            s_x = [sem(f"{nm}x{d}") for d in range(KT)]
            with nc.Block() as blk:
                @blk.sync
                def _(sp):
                    def load(g):
                        for half in range(2):
                            pr = slice(HD * half, HD * half + HD)
                            w = a["w_out"][l]
                            n_c = slice(g * P, (g + 1) * P)
                            for t0, n, r0, step in ((O_NA, 2, HD * half, P), (O_GA, 4, 256 + 256 * half, HD),
                                                    (O_WA, 2, 768 + P * half, HD)):
                                src = w[r0:r0 + (n - 1) * step + HD, n_c]
                                src = (src.rearrange("(k p) c -> p k c", p=HD) if step == HD
                                       else w[0:256, n_c].rearrange("(k p) c -> p k c", p=P)[HD * half:HD * half + HD])
                                sp.dma_start(w_raw[pr, g % 2, t0:t0 + n, :], src).then_inc(t.raw[g % 2], 16)
                    load(0)
                    load(1)
                    for d in range(KT):
                        sp.dma_start(x[:, d, 0:toks], x_spill.ap()[:, d, 0:toks]).then_inc(s_x[d], 16)
                    for g in range(2, KT):
                        sp.wait_ge(t.lo, g - 1)
                        load(g)

                @blk.scalar
                def _(act):
                    for g in range(KT):
                        act.wait_ge(t.raw[g % 2], 96 * (g // 2 + 1))
                        if g >= 2:
                            act.wait_ge(t.mm, t.n * (g - 1))
                        act.activation(w_hi[:, g % 2], w_raw[:, g % 2], ACT.Copy).then_inc(t.hi, 1)

                @blk.tensor
                def _(pe):
                    for g in range(KT):
                        t.multiply(pe, g // 2, g % 2, o_hi, o_lo, first=g < 2)

                @blk.vector
                def _(dve):
                    t.split_lo(dve, 0, 0)
                    t.split_lo(dve, 0, 1)
                    for g in range(KT):
                        dve.wait_ge(s_x[g], 16)
                        for c, (t0, n) in enumerate(chunks):
                            dve.wait_ge(t.mm, t.n * g + c + 1)
                            v = 0 if t0 < SEQ else 1
                            dve.scalar_tensor_tensor(out=x[:, g, t0:t0 + n], in0=ps[:, 3 * (g % 2) + c, 0:n],
                                                     scalar=modv[:, l * 48 + 2 * KT + g, v:v + 1],
                                                     in1=x[:, g, t0:t0 + n], op0=ALU.mult, op1=ALU.add)\
                                .then_inc(t.out, 1)
                        if g + 2 < KT:
                            t.split_lo(dve, g // 2 + 1, g % 2)

        def feed_forward(l, toks):
            nm = f"f{l}_"
            (s_ra, s_rb, s_rd, s_ahi, s_alo, s_bhi, s_blo, s_dhi, s_dlo, s_up, s_dn, s_ae, s_cv, s_sg, s_um,
             s_uh, s_ul, s_xu, s_ze) = [sem(nm + n) for n in (
                 "ra", "rb", "rd", "ahi", "alo", "bhi", "blo", "dhi", "dlo", "up", "dn", "ae", "cv", "sg", "um",
                 "uh", "ul", "xu", "ze")]
            chunks = [c for c in CHUNKS if c[0] < toks]
            nch = len(chunks)
            at_ = [t0 if t0 < SEQ else t0 + 1 for t0, _ in chunks]
            CW = SEQ if toks == SEQ else TOK + 1
            NP_ = KT * nch
            PER = NP_ // (2 * nch)
            wup = a["w_up"][l].rearrange("(k p) n -> p k n", p=P)
            wdn = a["w_down"][l]

            def steps(eng, body):
                body(0, 0)
                body(1, 1)
                with eng.Fori(1, FT // 2 - 1) as i:
                    for s in range(2):
                        body(2 * i + s, s)
                body(FT - 2, 0)
                body(FT - 1, 1, last=True)

            with nc.Block() as blk:
                @blk.gpsimd
                def _(g):
                    zc = [0, SEQ + 1] + ([TOK + 2] if toks > SEQ else [])
                    for c in zc:
                        g.memset(a_pad[:, c:c + 1], 0.0).then_inc(s_ze, 1)

                @blk.sync
                def _(sp):
                    def load(j):
                        c = (bass.ds(j * P, P) if not isinstance(j, int) else slice(j * P, j * P + P))
                        cb = (bass.ds(j * P + F, P) if not isinstance(j, int) else slice(F + j * P, F + j * P + P))
                        return c, cb

                    def body(j, s, last=False):
                        if last:
                            return
                        c, cb = load(j + 1)
                        sp.wait_ge(s_alo, j + 1)
                        sp.dma_start(w_raw[:, 0], wup[:, :, c]).then_inc(s_ra, 16)
                        sp.wait_ge(s_blo, j + 1)
                        sp.dma_start(w_raw[:, 1], wup[:, :, cb]).then_inc(s_rb, 16)
                        sp.wait_ge(s_dlo, j + 1)
                        sp.dma_start(wd_raw[:, :], wdn[c, :]).then_inc(s_rd, 16)
                    sp.dma_start(w_raw[:, 0], wup[:, :, 0:P]).then_inc(s_ra, 16)
                    sp.dma_start(w_raw[:, 1], wup[:, :, F:F + P]).then_inc(s_rb, 16)
                    sp.dma_start(wd_raw[:, :], wdn[0:P, :]).then_inc(s_rd, 16)
                    steps(sp, body)

                @blk.tensor
                def _(pe):
                    def down(j, r, ms):
                        for m_ in ms:
                            if m_ == 0:
                                pe.wait_ge(s_ul, nch * j + nch)
                                pe.wait_ge(s_dlo, j + 1)
                            if not (isinstance(j, int) and j == 0 and m_ < 2):
                                pe.wait_ge(s_xu, NP_ * j + m_ - 1)
                            d, (t0, n) = m_ // nch, chunks[m_ % nch]
                            three_pass(pe, ps[:, 6 + m_ % 2, 0:n], [wd_hi[:, r, d * P:(d + 1) * P]],
                                       [wd_lo[:, r, d * P:(d + 1) * P]], [u_hi[:, r, t0:t0 + n]],
                                       [u_lo[:, r, t0:t0 + n]]).then_inc(s_dn, 1)

                    def body(j, s, last=False):
                        zero = isinstance(j, int) and j == 0
                        for q in range(2):
                            pe.wait_ge(s_alo if q == 0 else s_blo, j + 1)
                            for c, (t0, n) in enumerate(chunks):
                                if not zero:
                                    pe.wait_ge(s_ae if q == 0 else s_um, nch * (j - 1) + c + 1)
                                three_pass(pe, ps[:, 3 * q + c, 0:n], [w_hi[:, q, k, :] for k in range(KT)],
                                           [w_lo[:, q, k, :] for k in range(KT)],
                                           [h_hi[:, k, t0:t0 + n] for k in range(KT)],
                                           [h_lo[:, k, t0:t0 + n] for k in range(KT)]).then_inc(s_up, 1)
                                if not zero:
                                    m0 = (q * nch + c) * PER
                                    down(j - 1, 1 - s, range(m0, m0 + PER))
                        if last:
                            down(j, s, range(NP_))
                    steps(pe, body)

                @blk.scalar
                def _(act):
                    def split(dst, src, loaded, done, j):
                        act.wait_ge(loaded, 16 * j + 16)
                        act.activation(dst, src, ACT.Copy).then_inc(done, 1)

                    def body(j, s, last=False):
                        zero = isinstance(j, int) and j == 0
                        small = isinstance(j, int) and j < 2
                        for c, (t0, n) in enumerate(chunks):
                            act.wait_ge(s_up, 2 * nch * j + c + 1)
                            if c == 0 and not zero:
                                act.wait_ge(s_cv, 3 * j)
                            act.activation(a_pad[:, at_[c] + 1:at_[c] + 1 + n], ps[:, c, 0:n], ACT.Copy)\
                                .then_inc(s_ae, 1)
                        if not last:
                            act.wait_ge(s_up, 2 * nch * j + nch)
                            split(w_hi[:, 0], w_raw[:, 0], s_ra, s_ahi, j + 1)
                        if not small:
                            act.wait_ge(s_dn, NP_ * (j - 1))
                        split(wd_hi[:, s, :], wd_raw[:, :], s_rd, s_dhi, j)
                        act.wait_ge(s_cv, 3 * j + 3)
                        if not zero:
                            act.wait_ge(s_ul, nch * j)
                        act.activation(gate[:, 0:CW], conv[:, 0:CW], ACT.Silu).then_inc(s_sg, 1)
                        for c, (t0, n) in enumerate(chunks):
                            act.wait_ge(s_um, nch * j + c + 1)
                            act.activation(u_hi[:, s, t0:t0 + n], gate[:, at_[c]:at_[c] + n], ACT.Copy)\
                                .then_inc(s_uh, 1)
                        if not last:
                            act.wait_ge(s_up, 2 * nch * (j + 1))
                            split(w_hi[:, 1], w_raw[:, 1], s_rb, s_bhi, j + 1)
                    split(w_hi[:, 0], w_raw[:, 0], s_ra, s_ahi, 0)
                    split(w_hi[:, 1], w_raw[:, 1], s_rb, s_bhi, 0)
                    steps(act, body)

                @blk.vector
                def _(dve):
                    def split(dst, src, hi, ready, done, j):
                        dve.wait_ge(ready, j + 1)
                        dve.tensor_tensor(dst, src, hi.bitcast(F32), ALU.subtract).then_inc(done, 1)

                    def update(j, ms):
                        for m_ in ms:
                            d, (t0, n) = m_ // nch, chunks[m_ % nch]
                            v = 0 if t0 < SEQ else 1
                            dve.wait_ge(s_dn, NP_ * j + m_ + 1)
                            if m_ == 0 and not (isinstance(j, int) and j == 0):
                                dve.wait_ge(s_xu, NP_ * j)
                            dve.scalar_tensor_tensor(out=x[:, d, t0:t0 + n], in0=ps[:, 6 + m_ % 2, 0:n],
                                                     scalar=modv[:, l * 48 + 5 * KT + d, v:v + 1],
                                                     in1=x[:, d, t0:t0 + n], op0=ALU.mult, op1=ALU.add)\
                                .then_inc(s_xu, 1)

                    def wcol(stage_no, row):
                        return vec[:, stage_no, (bass.ds(row, 1) if not isinstance(row, int) else slice(row, row + 1))]

                    def low(j, s, c):
                        t0, n = chunks[c]
                        dve.wait_ge(s_uh, nch * j + c + 1)
                        dve.tensor_tensor(u_lo[:, s, t0:t0 + n], gate[:, at_[c]:at_[c] + n],
                                          u_hi[:, s, t0:t0 + n].bitcast(F32), ALU.subtract).then_inc(s_ul, 1)

                    def body(j, s, last=False):
                        zero = isinstance(j, int) and j == 0
                        if not zero:
                            update(j - 1, range(PER * nch))
                        dve.wait_ge(s_ae, nch * j + nch)
                        if not zero:
                            dve.wait_ge(s_sg, j)
                        dve.tensor_scalar(conv[:, 0:CW], a_pad[:, 1:1 + CW], wcol(2 + l, j + FT),
                                          wcol(1, j + (32 + l * FT)), ALU.mult, ALU.add).then_inc(s_cv, 1)
                        dve.wait_ge(s_cv, 3 * j + 1)
                        dve.scalar_tensor_tensor(out=conv[:, 0:CW], in0=a_pad[:, 0:CW], scalar=wcol(2 + l, j),
                                                 in1=conv[:, 0:CW], op0=ALU.mult, op1=ALU.add).then_inc(s_cv, 1)
                        dve.wait_ge(s_cv, 3 * j + 2)
                        dve.scalar_tensor_tensor(out=conv[:, 0:CW], in0=a_pad[:, 2:2 + CW],
                                                 scalar=wcol(2 + l, j + 2 * FT), in1=conv[:, 0:CW],
                                                 op0=ALU.mult, op1=ALU.add).then_inc(s_cv, 1)
                        if not last:
                            split(w_lo[:, 0], w_raw[:, 0], w_hi[:, 0], s_ahi, s_alo, j + 1)
                        split(wd_lo[:, s, :], wd_raw[:, :], wd_hi[:, s, :], s_dhi, s_dlo, j)
                        dve.wait_ge(s_sg, j + 1)
                        for c, (t0, n) in enumerate(chunks):
                            if not zero:
                                m0 = (nch + c) * PER
                                update(j - 1, range(m0, m0 + PER))
                            if c >= 1:
                                low(j, s, c - 1)
                            dve.wait_ge(s_up, nch * (2 * j + 1) + c + 1)
                            dve.tensor_tensor(gate[:, at_[c]:at_[c] + n], ps[:, 3 + c, 0:n],
                                              gate[:, at_[c]:at_[c] + n], ALU.mult).then_inc(s_um, 1)
                        low(j, s, nch - 1)
                        if not last:
                            split(w_lo[:, 1], w_raw[:, 1], w_hi[:, 1], s_bhi, s_blo, j + 1)
                        else:
                            update(j, range(NP_))
                    dve.wait_ge(s_ze, 3 if toks > SEQ else 2)
                    split(w_lo[:, 0], w_raw[:, 0], w_hi[:, 0], s_ahi, s_alo, 0)
                    split(w_lo[:, 1], w_raw[:, 1], w_hi[:, 1], s_bhi, s_blo, 0)
                    steps(dve, body)

        with Phase():
            load()
        for l in range(DEPTH):
            last = l == DEPTH - 1
            toks = SEQ if last else TOK
            with Phase():
                norm(l, 0, TOK, spill=True)
            with Phase():
                project_in(l)
            for kind in (NA, WA, GA):
                with Phase():
                    attention(l, kind, toks // P)
            with Phase():
                project_out(l, toks)
            with Phase():
                norm(l, 1, toks)
            with Phase():
                feed_forward(l, toks)
        with Phase():
            norm(DEPTH, 0, SEQ, final=True)


_INS = ["x", "c", "ctx", "c_ctx", "attn_norm", "ffn_norm", "w_mod", "b_mod", "w_in", "q_gain", "k_gain",
        "na_rpb", "wa_sink", "w_out", "w_up", "conv_w", "conv_b", "w_down", "final_norm"]


def kernel(**inputs):
    import concourse.bacc as _bacc
    from concourse.bass_utils import run_bass_kernel_spmd as _run

    nc = _bacc.Bacc("TRN2", target_bir_lowering=False, num_devices=1)
    arrays, args = {}, {}
    for name in _INS:
        v = np.ascontiguousarray(inputs[name])
        if name in ("x", "ctx"):
            v = v.reshape(v.shape[1:])
        arrays[f"in_{name}"] = v
        args[name] = nc.dram_tensor(f"in_{name}", v.shape, F32, kind="ExternalInput").ap()
    arrays["in_consts"] = shape_constants()
    args["consts"] = nc.dram_tensor("in_consts", (P, N_CONST), F32, kind="ExternalInput").ap()
    args["out"] = nc.dram_tensor("out_x", (SEQ, D), F32, kind="ExternalOutput").ap()
    program(nc, args)
    r = _run(nc, [arrays], core_ids=[0])
    return r.results[0]["out_x"].reshape(1, SEQ, D)
```
